# Optimizing a Trainium2 kernel written in Bass

```python
import functools
import jax, jax.numpy as jnp
from jax import lax
import numpy as np

D_MODEL = 1024
BATCH = 1
SEQ = 256
DEPTH = 2
DEC_BATCH = 8
DEC_SEQ = 1
PAST_LEN = 1024
PAGE_SIZE = 128

CONV_W = D_MODEL // 4
CONV_K = 31
POOL_W = D_MODEL // 4
POOL_WINDOWS = (2, 4, 8, 16)
POOL_GROUPS = len(POOL_WINDOWS)
POOL_GW = POOL_W // POOL_GROUPS
POOL_BUF = max(POOL_WINDOWS) - 1
HEAD_DIM = 64
ATTN_W = D_MODEL - CONV_W - POOL_W
N_HEADS = ATTN_W // HEAD_DIM
N_KV_HEADS = 2
IDX_HEADS = 4
IDX_DIM = 64
INDEX_TOPK = 256
ROPE_THETA = 500000.0
ROPE_FRAC = 4
Q_BLOCK = 128
D_FF = 2816
D_MIX = CONV_W + POOL_W + ATTN_W
NORM_EPS = 1e-6
IN_SPLITS = (2 * CONV_W, POOL_W, ATTN_W, N_KV_HEADS * HEAD_DIM, N_KV_HEADS * HEAD_DIM,
             IDX_HEADS * IDX_DIM, IDX_DIM, IDX_HEADS)
D_IN = sum(IN_SPLITS)

kernel_name = 'hymba_conv_pool_dsa_decoder_step'

def rmsnorm(x, g):
    xf = x.astype(jnp.float32)
    y = xf * lax.rsqrt(jnp.mean(xf * xf, axis=-1, keepdims=True) + NORM_EPS)
    return (y * g.astype(jnp.float32)).astype(x.dtype)

def layernorm(x, g, b):
    xf = x.astype(jnp.float32)
    mu = jnp.mean(xf, axis=-1, keepdims=True)
    var = jnp.mean(jnp.square(xf - mu), axis=-1, keepdims=True)
    y = (xf - mu) * lax.rsqrt(var + NORM_EPS)
    return (y * g.astype(jnp.float32) + b.astype(jnp.float32)).astype(x.dtype)

def swiglu(x, wg, wu, wd):
    return (jax.nn.silu(x @ wg) * (x @ wu)) @ wd

def partial_rope(x, pos):
    rot = x.shape[-1] // ROPE_FRAC
    half = rot // 2
    inv = ROPE_THETA ** (-jnp.arange(half, dtype=jnp.float32) * 2.0 / rot)
    ang = pos.astype(jnp.float32)[:, None] * inv[None, :]
    cos = jnp.cos(ang)[:, None, :]
    sin = jnp.sin(ang)[:, None, :]
    xf = x.astype(jnp.float32)
    x1, x2 = xf[..., :half], xf[..., half:rot]
    out = jnp.concatenate([x1 * cos - x2 * sin, x2 * cos + x1 * sin, xf[..., rot:]], axis=-1)
    return out.astype(x.dtype)

def conv_mixer(a, prev, dw, dw_bias, ln_g, ln_b, pw):
    g = a[..., :CONV_W] * jax.nn.sigmoid(a[..., CONV_W:])
    buf = jnp.concatenate([prev.astype(g.dtype), g], axis=1)
    y = lax.conv_general_dilated(buf, dw[:, None, :].astype(g.dtype), window_strides=(1,),
                                 padding='VALID', dimension_numbers=('NWC', 'WIO', 'NWC'),
                                 feature_group_count=CONV_W) + dw_bias
    y = jax.nn.silu(layernorm(y, ln_g, ln_b)) @ pw
    return y, buf[:, -(CONV_K - 1):]

def pool_mixer(xb, prev, pos, pool_w, pool_scale):
    B, T, _ = xb.shape
    buf = jnp.concatenate([prev.astype(xb.dtype), xb], axis=1)
    xf = buf.astype(jnp.float32)
    cs = jnp.concatenate([jnp.zeros((B, 1, POOL_W), jnp.float32), jnp.cumsum(xf, axis=1)], axis=1)
    hi = POOL_BUF + 1 + jnp.arange(T)
    means = []
    for g, w in enumerate(POOL_WINDOWS):
        c = slice(g * POOL_GW, (g + 1) * POOL_GW)
        cnt = jnp.minimum(w, pos + 1).astype(jnp.float32)
        means.append((cs[:, hi, c] - cs[:, hi - w, c]) / cnt[None, :, None])
    pooled = (jnp.concatenate(means, axis=-1) - xf[:, POOL_BUF:]).astype(xb.dtype)
    y = jnp.einsum('btgc,gcd->btgd', pooled.reshape(B, T, POOL_GROUPS, POOL_GW), pool_w)
    y = y.reshape(B, T, POOL_W) * pool_scale
    return y, buf[:, -POOL_BUF:]

def indexer_scores(qi, wi, ki):
    d = jnp.einsum('bthd,bsd->bths', qi.astype(jnp.float32), ki.astype(jnp.float32)) * IDX_DIM ** -0.5
    return jnp.einsum('bths,bth->bts', jax.nn.relu(d), wi.astype(jnp.float32) * IDX_HEADS ** -0.5)

def sparse_attend(q, ks, vs, valid):
    B, T = q.shape[:2]
    qg = q.reshape(B, T, N_KV_HEADS, N_HEADS // N_KV_HEADS, HEAD_DIM).astype(jnp.float32)
    s = jnp.einsum('btngd,btknd->btngk', qg, ks.astype(jnp.float32)) * HEAD_DIM ** -0.5
    s = jnp.where(valid[:, :, None, None, :], s, -jnp.inf)
    p = jax.nn.softmax(s, axis=-1)
    o = jnp.einsum('btngk,btknd->btngd', p, vs.astype(jnp.float32))
    return o.reshape(B, T, ATTN_W).astype(q.dtype)

def gather_rows(rows, idx):
    return jax.vmap(lambda r, i: r[i])(rows, idx)

def dsa_prompt(q, k, v, qi, ki, wi, pos):
    B, T = q.shape[:2]
    topk = min(INDEX_TOPK, T // 4)
    nb = T // Q_BLOCK

    def to_blocks(t):
        return t.reshape((B, nb, Q_BLOCK) + t.shape[2:]).swapaxes(0, 1)

    def block(args):
        qb, qib, wb, pb = args
        sc = indexer_scores(qib, wb, ki)
        sc = jnp.where(pos[None, None, :] <= pb[None, :, None], sc, -jnp.inf)
        _, sel = lax.top_k(sc, topk)
        valid = sel <= pb[None, :, None]
        return sparse_attend(qb, gather_rows(k, sel), gather_rows(v, sel), valid)

    out = lax.map(block, (to_blocks(q), to_blocks(qi), to_blocks(wi), pos.reshape(nb, Q_BLOCK)))
    return out.swapaxes(0, 1).reshape(B, T, ATTN_W)

def dsa_sample(q, k, v, qi, ki, wi, pos, cache_k, cache_v, cache_kidx, page_table):
    B, T = q.shape[:2]
    past = page_table.shape[1] * PAGE_SIZE
    topk = min(INDEX_TOPK, (past + T) // 4)
    ki_past = cache_kidx[page_table].reshape(B, past, IDX_DIM)
    ki_all = jnp.concatenate([ki_past.astype(ki.dtype), ki], axis=1)
    sc = indexer_scores(qi, wi, ki_all)
    kpos = jnp.arange(past + T)
    sc = jnp.where(kpos[None, None, :] <= pos[None, :, None], sc, -jnp.inf)
    _, sel = lax.top_k(sc, topk)
    valid = sel <= pos[None, :, None]
    is_new = sel >= past
    old_idx = jnp.minimum(sel, past - 1)
    phys = jnp.take_along_axis(page_table, (old_idx // PAGE_SIZE).reshape(B, -1), axis=1).reshape(sel.shape)
    off = old_idx % PAGE_SIZE
    new_idx = jnp.clip(sel - past, 0, T - 1)

    def gather(cache, new):
        old = cache[phys, off].astype(new.dtype)
        return jnp.where(is_new[..., None, None], gather_rows(new, new_idx), old)

    return sparse_attend(q, gather(cache_k, k), gather(cache_v, v), valid)

def token_mixing(u, pos, conv_prev, pool_prev, w_in, conv_dw, conv_dw_bias, conv_ln_gain, conv_ln_bias,
                 conv_pw, pool_w, pool_scale, w_out, attend):
    B, T, _ = u.shape
    a = u @ w_in
    offs = [int(o) for o in np.cumsum(IN_SPLITS)[:-1]]
    a_conv, a_pool, a_q, a_k, a_v, a_qi, a_ki, a_wi = jnp.split(a, offs, axis=-1)
    q = partial_rope(a_q.reshape(B, T, N_HEADS, HEAD_DIM), pos)
    k = partial_rope(a_k.reshape(B, T, N_KV_HEADS, HEAD_DIM), pos)
    v = a_v.reshape(B, T, N_KV_HEADS, HEAD_DIM)
    qi = partial_rope(a_qi.reshape(B, T, IDX_HEADS, IDX_DIM), pos)
    ki = partial_rope(a_ki.reshape(B, T, 1, IDX_DIM), pos)[:, :, 0]
    y_c, conv_state = conv_mixer(a_conv, conv_prev, conv_dw, conv_dw_bias, conv_ln_gain, conv_ln_bias, conv_pw)
    y_p, pool_state = pool_mixer(a_pool, pool_prev, pos, pool_w, pool_scale)
    y_a = attend(q, k, v, qi, ki, a_wi, pos)
    y = jnp.concatenate([y_c, y_p, y_a], axis=-1) @ w_out
    return y, (k, v, ki, conv_state, pool_state)

def macaron_ffn(x, p):
    npre, wg, wu, wd, npost = p
    return x + 0.5 * rmsnorm(swiglu(rmsnorm(x, npre), wg, wu, wd), npost)

def layer(x, pos, conv_prev, pool_prev, lp, attend):
    h = macaron_ffn(x, lp['ffn1'])
    npre, mix_w, npost = lp['mix']
    y, state = token_mixing(rmsnorm(h, npre), pos, conv_prev, pool_prev, *mix_w, attend)
    h = h + rmsnorm(y, npost)
    h = macaron_ffn(h, lp['ffn2'])
    return h, state

def setup_inputs(seed: int = 0) -> dict:
    key = jax.random.key(seed)
    ks = iter(jax.random.split(key, 40))
    n_pages = PAST_LEN // PAGE_SIZE
    n_phys = (DEC_BATCH * n_pages * 5) // 4

    def nrm(shape, scale):
        return jax.random.normal(next(ks), shape, jnp.float32) * scale

    def gain(shape, s=0.02):
        return 1.0 + nrm(shape, s)

    d = {}
    d['x_prompt'] = nrm((BATCH, SEQ, D_MODEL), 1.0)
    d['x_sample'] = nrm((DEC_BATCH, DEC_SEQ, D_MODEL), 1.0)
    d['cache_k'] = nrm((DEPTH, n_phys, PAGE_SIZE, N_KV_HEADS, HEAD_DIM), 1.0)
    d['cache_v'] = nrm((DEPTH, n_phys, PAGE_SIZE, N_KV_HEADS, HEAD_DIM), 1.0)
    d['cache_kidx'] = nrm((DEPTH, n_phys, PAGE_SIZE, IDX_DIM), 1.0)
    d['state_conv'] = nrm((DEPTH, DEC_BATCH, CONV_K - 1, CONV_W), 1.0)
    d['state_pool'] = nrm((DEPTH, DEC_BATCH, POOL_BUF, POOL_W), 1.0)
    perm = jax.random.permutation(next(ks), n_phys)[: DEC_BATCH * n_pages]
    d['page_table'] = perm.reshape(DEC_BATCH, n_pages).astype(jnp.int32)
    d['ffn1_norm_pre'] = gain((DEPTH, D_MODEL))
    d['ffn1_w_gate'] = nrm((DEPTH, D_MODEL, D_FF), D_MODEL ** -0.5)
    d['ffn1_w_up'] = nrm((DEPTH, D_MODEL, D_FF), D_MODEL ** -0.5)
    d['ffn1_w_down'] = nrm((DEPTH, D_FF, D_MODEL), D_FF ** -0.5)
    d['ffn1_norm_post'] = gain((DEPTH, D_MODEL))
    d['mix_norm_pre'] = gain((DEPTH, D_MODEL))
    d['w_in'] = nrm((DEPTH, D_MODEL, D_IN), D_MODEL ** -0.5)
    d['conv_dw'] = nrm((DEPTH, CONV_K, CONV_W), CONV_K ** -0.5)
    d['conv_dw_bias'] = nrm((DEPTH, CONV_W), 0.01)
    d['conv_ln_gain'] = gain((DEPTH, CONV_W))
    d['conv_ln_bias'] = nrm((DEPTH, CONV_W), 0.01)
    d['conv_pw'] = nrm((DEPTH, CONV_W, CONV_W), CONV_W ** -0.5)
    d['pool_w'] = nrm((DEPTH, POOL_GROUPS, POOL_GW, POOL_GW), POOL_GW ** -0.5)
    d['pool_scale'] = gain((DEPTH, POOL_W), 0.1)
    d['w_out'] = nrm((DEPTH, D_MIX, D_MODEL), D_MIX ** -0.5)
    d['mix_norm_post'] = gain((DEPTH, D_MODEL))
    d['ffn2_norm_pre'] = gain((DEPTH, D_MODEL))
    d['ffn2_w_gate'] = nrm((DEPTH, D_MODEL, D_FF), D_MODEL ** -0.5)
    d['ffn2_w_up'] = nrm((DEPTH, D_MODEL, D_FF), D_MODEL ** -0.5)
    d['ffn2_w_down'] = nrm((DEPTH, D_FF, D_MODEL), D_FF ** -0.5)
    d['ffn2_norm_post'] = gain((DEPTH, D_MODEL))
    return d

def reference(x_prompt, x_sample, cache_k, cache_v, cache_kidx, state_conv, state_pool, page_table,
              ffn1_norm_pre, ffn1_w_gate, ffn1_w_up, ffn1_w_down, ffn1_norm_post,
              mix_norm_pre, w_in, conv_dw, conv_dw_bias, conv_ln_gain, conv_ln_bias, conv_pw,
              pool_w, pool_scale, w_out, mix_norm_post,
              ffn2_norm_pre, ffn2_w_gate, ffn2_w_up, ffn2_w_down, ffn2_norm_post):
    Bp, Tp = x_prompt.shape[:2]
    Bs, Ts = x_sample.shape[:2]
    past = page_table.shape[1] * PAGE_SIZE
    pos_p = jnp.arange(Tp)
    pos_s = past + jnp.arange(Ts)
    conv0 = jnp.zeros((Bp, CONV_K - 1, CONV_W), x_prompt.dtype)
    pool0 = jnp.zeros((Bp, POOL_BUF, POOL_W), x_prompt.dtype)
    hp, hs = x_prompt, x_sample
    sp = ([], [], [], [], [])
    ss = ([], [], [], [], [])
    for l in range(DEPTH):
        lp = {
            'ffn1': (ffn1_norm_pre[l], ffn1_w_gate[l], ffn1_w_up[l], ffn1_w_down[l], ffn1_norm_post[l]),
            'mix': (mix_norm_pre[l],
                    (w_in[l], conv_dw[l], conv_dw_bias[l], conv_ln_gain[l], conv_ln_bias[l], conv_pw[l],
                     pool_w[l], pool_scale[l], w_out[l]),
                    mix_norm_post[l]),
            'ffn2': (ffn2_norm_pre[l], ffn2_w_gate[l], ffn2_w_up[l], ffn2_w_down[l], ffn2_norm_post[l]),
        }
        attend_s = functools.partial(dsa_sample, cache_k=cache_k[l], cache_v=cache_v[l],
                                     cache_kidx=cache_kidx[l], page_table=page_table)
        hp, st_p = layer(hp, pos_p, conv0, pool0, lp, dsa_prompt)
        hs, st_s = layer(hs, pos_s, state_conv[l], state_pool[l], lp, attend_s)
        for acc, val in zip(sp, st_p):
            acc.append(val)
        for acc, val in zip(ss, st_s):
            acc.append(val)
    return (hp, hs,
            jnp.stack(sp[0]), jnp.stack(sp[1]), jnp.stack(sp[2]), jnp.stack(sp[3]), jnp.stack(sp[4]),
            jnp.stack(ss[0]), jnp.stack(ss[1]), jnp.stack(ss[2]), jnp.stack(ss[3]), jnp.stack(ss[4]))


_drawn_inputs = setup_inputs


def setup_inputs(seed=0):
    import zlib

    import numpy as np

    out = dict(_drawn_inputs(seed))
    spreads = {}
    factors = {'conv_dw_bias': 3.447,
     'conv_ln_gain': 3.178,
     'conv_ln_bias': 5.931,
     'ffn2_norm_pre': 3.279,
     'ffn2_norm_post': 4.227}
    for name, (base, spread) in spreads.items():
        noise = np.random.default_rng([zlib.crc32(name.encode()), seed]).standard_normal(out[name].shape)
        drawn = base * np.exp(spread * noise) if base else spread * noise
        out[name] = __import__('jax').numpy.asarray(drawn.astype(out[name].dtype))
    for name, factor in factors.items():
        out[name] = (out[name] * factor).astype(out[name].dtype)
    return out
```

```python
from contextlib import ExitStack

import numpy as np
import concourse.bass as bass
from concourse import mybir

F32, F32R, I32 = mybir.dt.float32, mybir.dt.float32r, mybir.dt.int32
AL = mybir.AluOpType
ACT = mybir.ActivationFunctionType
AX = mybir.AxisListType

D, DFF, DEPTH = 1024, 2816, 2
NP, NB = 256, 8
NT = NP + NB
KD, KF = D // 128, DFF // 128
HD, NH, IH = 64, 8, 4
PAGE, NPG = 128, 8
PAST = PAGE * NPG
TOPK_P, TOPK_S = 64, 256
CK, PB = 31, 15
EPS = 1e-6
SCALE = HD ** -0.5

U_FFN = 3 * KF
N_IN, N_OUT = 16, 8
U_MIX = U_FFN
U_FFN2 = U_MIX + N_IN + N_OUT
UNITS = U_FFN2 + U_FFN
RAW, SPLIT, KV = 6, 3, 4
TAIL = 2

PRE1, POST1, PREM, POSTM, PRE2, POST2, PRE1N = (8 * i for i in range(7))
DW = 56
DWB, LNG, LNB, PSC = DW + 2 * CK, DW + 2 * CK + 2, DW + 2 * CK + 4, DW + 2 * CK + 6
NPAR = PSC + 2

C_ID, C_PERM, C_DUP, C_DUPP, C_SWAP, C_ONE = (128 * i for i in range(6))
C_COS = 768
C_SIN = C_COS + NT
C_CNT = C_SIN + NT
C_CA0 = C_CNT + 2 * NT
C_CA1 = C_CA0 + 128
C_WIM = C_CA1 + 256
C_WXM = C_WIM + 32
NCONST = C_WXM + 64

DBG = 1
BIG = 1e30
TAKEN = -2e38

SIGNALS = dict(
    w_hi=UNITS, w_lo=UNITS, unit_done=UNITS,
    gs=2 * KF, silu=2 * KF, us=2 * KF, mid=2 * KF, h_hi=2 * KF, h_lo=2 * KF,
    y_done=14, y_out=24, sq_post=24, mm_post=24, rms_post=3, h_new=24,
    x_hi=24, x_lo=24, sq_pre=24, mm_pre=24, rms_pre=3, rstd=3,
    chunk=15, perm=8, rope=8, wi_t=1, wi_mask=1, wi_x=1, wi_w=1, swap=1, lq=1,
    idx_p=4, idx_relu=4, v_t=1, v_nat=1, idx_d=1, idx_dr=1, idx_s=1, idx_x=1,
    mask_p=1, mask_s=1, la=1,
    s_p=4, s_masked=4, p_exp=4, p_norm=4, p_t=8, p_tc=8, o_p=4, o_hi=4, o_lo=4,
    s_s=1, s_smax=1, p_sexp=1, p_snorm=1, p_st=1, p_stc=1, k_used=8, v_used=8, o_sc=1, o_st=1, o_ms=1,
    o_shi=1, o_slo=1, dg=1,
    tanh=2, glu=2, conv=1, c_sum=1, c_cent=1, c_sq=1, c_var=1, c_rms=1, c_norm=1, c_silu=1,
    c_hi=1, c_lo=1, c_out=1, c_ohi=1, c_olo=1,
    pool_x=1, pool_y=1, pl_hi=1, pl_lo=1, pl_ohi=1, pl_olo=1,
    step=400, pstep=60, astep=40,
)
FIRST = dict(w_hi=2, w_lo=2, x_hi=8, x_lo=8, sq_pre=8, mm_pre=8, rms_pre=1, rstd=1,
             unit_done=1, gs=1, us=1, mid=1, h_lo=1)


def build(nc, xT, wts, par, cst, ptab, kT, vC, kxT, scT, spT,
          yT, okT, ovT, okiT, ocP, ocS, opP, opS):
    ctx = ExitStack()
    with ctx:
        at = [nc.sbuf_base + 64 - nc.sbuf_base % 64]

        def place(name, shape, dt, where=at):
            n = 4 * int(np.prod(shape[1:]))
            t = nc.alloc_sbuf_tensor_at(name, shape, dt, offset=where[0])
            where[0] += -(-n // 64) * 64
            assert where[0] <= nc.sbuf_usable_end, (name, where[0])
            return t

        raw = place("raw", [128, RAW, 1024], F32)
        w_hi = place("w_hi", [128, SPLIT, 1024], F32R)
        w_lo = place("w_lo", [128, SPLIT, 1024], F32R)
        h = place("h", [128, KD, NT], F32)
        x_hi = place("x_hi", [128, KD, NT], F32R)
        y_at = [at[0]]
        x_lo = place("x_lo", [128, KD, NT], F32R)
        y = place("y", [128, KD, NT], F32, y_at)
        s1 = [at[0] + 4 * KD * NT]
        h_hi = place("h_hi", [128, KF, NT], F32R)
        s1_end = at[0]
        s2 = [at[0] + 4 * KD * NT]
        h_lo = place("h_lo", [128, KF, NT], F32R)
        s2_end = at[0]
        s_sq = [at[0]]
        sq_post = place("sq_post", [128, 4, NT], F32)
        sq_pre = place("sq_pre", [128, 4, NT], F32)
        s_gs0, s_gs = at[0], [at[0]]
        gs = place("gs", [128, 3, NT], F32)
        us = place("us", [128, 3, NT], F32)
        gs_end = at[0]
        rstd_post = place("rstd_post", [128, NT], F32)
        rstd = place("rstd", [128, NT], F32)
        pars = place("pars", [128, NPAR], F32)
        con = place("con", [128, NCONST], F32)
        tab = place("tab", [1, NB * NPG], I32)
        epsb = place("epsb", [128, 1], F32)
        s_kx = [at[0]]
        kx = place("kx", [128, 4, PAST], F32)
        kx_end = at[0]
        kv = place("kv", [128, KV, PAST], F32)
        LA = place("LA", [128, NB, 64], F32)
        LQ = place("LQ", [128, 4, 32], F32)
        gp = place("gp", [128, 2, 30 + NP], F32)
        pp = place("pp", [128, 2, PB + NP], F32)
        osb = place("osb", [128, 2, 128], F32)
        stc = place("stc", [128, 2, NB, CK], F32)
        stp = place("stp", [128, 2, NB, PB + 1], F32)
        qi = place("qi", [128, 2, NT], F32, s1)
        ki = place("ki", [128, NT], F32, s1)
        aq = place("aq", [128, 4, NT], F32, s1)
        ak = place("ak", [128, NT], F32, s1)
        av = place("av", [128, NT], F32, s1)
        X = place("X", [64, PAST + 1], F32, s1)
        assert s1[0] <= s1_end
        relu = place("relu", [128, 4, 256], F32, s2)
        relu0 = place("relu0", [128, 4, 128], F32, s2)
        wk1 = place("wk1", [128, 256], F32, s2)
        wk0 = place("wk0", [128, 128], F32, s2)
        vn = place("vn", [128, 2, 128], F32, s2)
        kiw = place("kiw", [128, NT], F32, s2)
        rd = place("rd", [32, PAST + 1], F32, s2)
        assert s2[0] <= s2_end
        bias_s = place("bias_s", [64, PAST + 1], F32)
        rtmp = place("rtmp", [128, 2, NT], F32)
        wi = place("wi", [128, 2, IH], F32)
        w4 = place("w4", [128, 32], F32)
        wx = place("wx", [32, 64], F32)
        kn = place("kn", [128, 4], F32)
        best = place("best", [128, 8], F32)
        best0 = place("best0", [128, 8], F32)
        bests = place("bests", [64, 8], F32)
        bias1 = place("bias1", [128, 256], F32)
        bias0 = place("bias0", [128, 128], F32)
        sp_ = place("sp_", [128, 2, 2, 384], F32, s_kx)
        spm = place("spm", [128, 2, 4], F32)
        sps = place("sps", [128, 2, 4], F32)
        pT = place("pT", [128, 2, 384], F32, s_kx)
        psm = place("psm", [64, PAST + 1], F32, s_kx)
        smx = place("smx", [64, 4], F32)
        pTs = place("pTs", [128, NPG, 64], F32, s_kx)
        dg = place("dg", [64, 64], F32)
        t2 = place("t2", [128, NH, NB], F32)
        ms = place("ms", [128, 4, NB], F32)
        cv = place("cv", [128, 2, NT], F32)
        cg = place("cg", [128, 2, NT], F32)
        cacc = place("cacc", [128, 2, NT], F32, s_gs)
        csq = place("csq", [128, 2, NT], F32, s_sq)
        crs = place("crs", [128, NT], F32)
        ctmp = place("ctmp", [128, 2, NB, CK], F32)
        cp_hi = place("cp_hi", [128, 2, NT], F32R, s_gs)
        cp_lo = place("cp_lo", [128, 2, NT], F32R, s_gs)
        xp = place("xp", [128, 2, NT], F32, s_sq)
        pw = place("pw", [128, 2, NT], F32, s_sq)
        pa = place("pa", [128, PB + NP], F32)
        pb = place("pb", [128, PB + NP], F32)
        pl_hi = place("pl_hi", [128, 2, NT], F32R, s_sq)
        pl_lo = place("pl_lo", [128, 2, NT], F32R)

        if DBG: print("SBUF end", at[0], nc.sbuf_usable_end)
        assert s_kx[0] <= kx_end and s_gs[0] <= gs_end and s_sq[0] <= s_gs0

        PS = ctx.enter_context(nc.psum_tensor("PS", [128, 8, 512], F32))
        sem = {n: ctx.enter_context(nc.semaphore(n)) for n in SIGNALS}
        raw_full = [ctx.enter_context(nc.semaphore(f"raw_full{i}")) for i in range(RAW)]
        kv_full = [ctx.enter_context(nc.semaphore(f"kv_full{i}")) for i in range(KV)]
        setup, inputs, pars_full, kx_full, state_full, stored = (
            ctx.enter_context(nc.semaphore(n))
            for n in ("setup", "inputs", "pars_full", "kx_full", "state_full", "stored"))
        made = {}
        block = ctx.enter_context(nc.Block())

        ident = con[:, C_ID:C_ID + 128]
        ones = con[:, C_ONE:C_ONE + 128]

        def says(name, ins, turns=1):
            made[name] = made.get(name, 0) + turns
            return ins.then_inc(sem[name], 1)

        def counted():
            for name, n in made.items():
                assert SIGNALS[name] == n, (name, n)
            made.clear()

        def wait(e, L, name, k):
            e.wait_ge(sem[name], L * SIGNALS[name] + (k + FIRST.get(name, 0)))

        ffn_loop = (KF - 1) // 3

        @block.sync
        def _(sp):
            def unit(n, i=0):
                if not isinstance(i, int) or n >= RAW:
                    sp.wait_ge(sem["w_hi"], i * RAW + (n - RAW + 1))
                    sp.wait_ge(sem["w_lo"], i * RAW + (n - RAW + 1))
                src = wts[n] if isinstance(i, int) else \
                    wts[bass.ds(i * RAW + n, 1)].rearrange("a p n -> p (a n)")
                sp.dma_start(raw[:, n % RAW, :], src).then_inc(raw_full[n % RAW], 16)

            def page(n):
                return sp.value_load(tab[0:1, bass.ds(n, 1)], min_val=0, max_val=kT.shape[1] - 1)

            def cache(src, L, b, g):
                sp.dma_start(kv[:, b % KV, bass.ds(g * PAGE, PAGE)],
                             src[L, bass.ds(page(g + b * NPG), 1)].rearrange("b p n -> (b p) n")) \
                    .then_inc(kv_full[b % KV], 16)

            def batch(src, L, b, free):
                wait(sp, L, *free)
                with sp.Fori(0, NPG) as g:
                    cache(src, L, b, g)

            for n in range(RAW):
                unit(n)
            sp.wait_ge(inputs, 64)
            for L in range(DEPTH):
                n = L * UNITS + RAW
                with sp.Fori(0, NPG) as g:
                    for j in range(RAW):
                        unit(n + j, g)
                    for b in range(NB):
                        half = slice(64 * (b % 2), 64 * (b % 2) + 64)
                        sp.dma_start(kx[half, b // 2, bass.ds(g * PAGE, PAGE)],
                                     kxT[L, bass.ds(page(g + b * NPG), 1)].rearrange("b p n -> (b p) n")) \
                            .then_inc(kx_full, 16)
                n += NPG * RAW
                with sp.Fori(0, NPG // 2) as i:
                    for j in range(RAW):
                        unit(n + j, i)
                    for b in range(KV):
                        for g in range(2):
                            cache(kT, L, b, i * 2 + g)
                n += NPG // 2 * RAW
                end = L * UNITS + U_MIX + 21
                for n in range(n, end):
                    unit(n)
                for b in range(KV, NB):
                    batch(kT, L, b, ("k_used", b - KV + 1))
                for b in range(KV):
                    batch(vC, L, b, ("k_used", KV + b + 1))
                for n in range(end, L * UNITS + U_FFN2):
                    unit(n)
                for b in range(KV, NB):
                    batch(vC, L, b, ("v_used", b - KV + 1))
                n = L * UNITS + U_FFN2
                last = (L + 1) * UNITS + (RAW if L + 1 < DEPTH else TAIL)
                with sp.Fori(0, (last - n) // RAW) as i:
                    for j in range(RAW):
                        unit(n + j, i)
                for n in range(last - (last - n) % RAW, last):
                    unit(n)

        def raw_ready(e, L, u, i=0):
            e.wait_ge(raw_full[u % RAW], L * (16 * UNITS // RAW) + i * 16 + 16 * (u // RAW + 1))

        def split_free(e, L, u, i=0):
            wait(e, L, "unit_done", i * RAW + (u - SPLIT + 1))

        @block.scalar
        def _(act):
            def split(L, u, i=0, turns=1, first=False):
                raw_ready(act, L, u, i)
                if not first:
                    split_free(act, L, u, i)
                says("w_hi", act.activation(w_hi[:, u % SPLIT, :], raw[:, u % RAW, :], ACT.Copy), turns)

            def pre(L, k0, gain):
                for d in range(KD):
                    wait(act, L, "h_new", k0 + d + 1)
                    says("x_hi", act.activation(x_hi[:, d, :], h[:, d, :], ACT.Copy,
                                                scale=pars[:, gain + d:gain + d + 1]))
                    if d >= 4:
                        wait(act, L, "mm_pre", k0 + d - 3)
                    says("sq_pre", act.activation(sq_pre[:, d % 4, :], h[:, d, :], ACT.Square))
                wait(act, L, "mm_pre", k0 + KD)
                says("rms_pre", act.activation(rstd[:, :], PS[:, 7, 0:NT], ACT.Sqrt,
                                               scale=1.0 / D, bias=epsb[:, :]))

            def post(L, n, nxt):
                for d in range(KD):
                    if n == 1:
                        wait(act, L, "unit_done", U_MIX + N_IN + d + 1)
                    elif d < KD - 1:
                        wait(act, L, "y_done", 7 * (n // 2) + d + 1)
                    else:
                        wait(act, L, "unit_done", U_FFN if n == 0 else UNITS)
                    says("y_out", act.activation(y[:, d, :], PS[:, d, 0:NT], ACT.Copy))
                wait(act, L, "mm_post", 8 * n + 8)
                says("rms_post", act.activation(rstd_post[:, :], PS[:, 0, 0:NT], ACT.Sqrt,
                                                scale=1.0 / D, bias=epsb[:, :]))
                pre(L, 8 * n, nxt)

            def ffn(L, u0, f0):
                def silu(f, i=0, turns=1):
                    wait(act, L, "gs", i * 3 + (f0 + f + 1))
                    says("silu", act.activation(gs[:, f % 3, :], gs[:, f % 3, :], ACT.Silu), turns)

                def hi(f, k, i=0, turns=1):
                    wait(act, L, "mid", i * 3 + (f0 + f + 1))
                    out = h_hi[:, k, :] if isinstance(k, int) else h_hi[:, bass.ds(k, 1), :]
                    says("h_hi", act.activation(out, us[:, f % 3, :], ACT.Copy), turns)

                split(L, u0 + 2)
                silu(0)
                split(L, u0 + 3)
                with act.Fori(0, ffn_loop) as i:
                    for f in range(1, 4):
                        split(L, u0 + 2 * f + 2, i, ffn_loop)
                        silu(f, i, ffn_loop)
                        split(L, u0 + 2 * f + 3, i, ffn_loop)
                        hi(f - 1, i * 3 + (f - 1), i, ffn_loop)
                split(L, u0 + 46)
                hi(KF - 1, KF - 1)
                split(L, u0 + 47)
                with act.Fori(0, 3) as i:
                    for k in range(48, 54):
                        split(L, u0 + k, i, 3)
                split(L, u0 + 66)
                split(L, u0 + 67)

            def mixer(L):
                u0 = U_MIX

                def rope_ready():
                    pass

                for m in range(2, 8):
                    split(L, u0 + m)
                for n, (bank, out) in enumerate(((4, relu[:, 0:2, :]), (5, relu[:, 2:4, :]),
                                                 (6, relu0[:, 0:2, :]), (7, relu0[:, 2:4, :]))):
                    wait(act, L, "idx_p", n + 1)
                    says("idx_relu", act.activation(
                        out, PS[:, bank, 0:out.shape[1] * out.shape[2]].rearrange("p (a b) -> p a b", a=2),
                        ACT.Relu, scale=SCALE))
                wait(act, L, "v_t", 1)
                says("v_nat", act.activation(vn[:, :, :], PS[:, 3, 0:256].rearrange(
                    "p (a b) -> p a b", a=2), ACT.Copy))
                split(L, u0 + 8)
                wait(act, L, "idx_d", 1)
                act.activation(rd[:, 0:PAST], PS[0:32, 4:6, :].rearrange("p a b -> p (a b)"), ACT.Relu, scale=SCALE)
                says("idx_dr", act.activation(rd[:, PAST:], PS[0:32, 6, 0:1], ACT.Relu, scale=SCALE))
                for m in range(9, 13):
                    split(L, u0 + m)
                for c in range(2):
                    wait(act, L, "chunk", 11 + 2 * c)
                    says("tanh", act.activation(cg[:, c, :], cg[:, c, :], ACT.Tanh, scale=0.5))
                    if c == 0:
                        split(L, u0 + 13)
                        split(L, u0 + 14)
                for m in range(15, 18):
                    split(L, u0 + m)

                def exps(j):
                    wait(act, L, "s_masked", j + 1)
                    for a in range(2):
                        for b, (lo, hi) in enumerate(((0, 256), (256, 384))):
                            t = sp_[:, j % 2, a, lo:hi]
                            ins = act.activation(t, t, ACT.Exp, scale=SCALE,
                                                 bias=spm[:, j % 2, 2 * a + b:2 * a + b + 1],
                                                 accum_out=sps[:, j % 2, 2 * a + b:2 * a + b + 1])
                    says("p_exp", ins)

                exps(0)
                exps(1)
                for j in range(4):
                    for a in range(2):
                        wait(act, L, "p_t", 2 * j + a + 1)
                        if j:
                            wait(act, L, "o_p", j)
                        says("p_tc", act.activation(pT[:, a, :], PS[:, 6 + a, 0:384], ACT.Copy))
                    wait(act, L, "o_p", j + 1)
                    says("o_hi", act.activation(h_hi[:, 4 + j, 0:NP], PS[:, j % 2, 0:NP], ACT.Copy))
                    if j < 2:
                        exps(j + 2)
                wait(act, L, "s_smax", 1)
                says("p_sexp", act.activation(psm[:, :], psm[:, :], ACT.Exp, scale=SCALE,
                                              bias=smx[:, 1:2], accum_out=smx[:, 2:3]))
                wait(act, L, "p_st", 1)
                says("p_stc", act.activation(pTs[:, :, :], PS[:, 7, :].rearrange(
                    "p (a b) -> p a b", a=NPG), ACT.Copy))
                wait(act, L, "v_used", NB)
                for q in range(4):
                    ins = act.activation(osb[32 * q:32 * q + 8, :, :], PS[32 * q:32 * q + 8, 2:4, 0:128], ACT.Copy)
                says("o_sc", ins)
                wait(act, L, "o_ms", 1)
                says("o_shi", act.activation(h_hi[:, 4:8, NP:], ms[:, :, :], ACT.Copy))
                wait(act, L, "c_cent", 1)
                says("c_sq", act.activation(csq[:, :, :], cacc[:, :, :], ACT.Square))
                wait(act, L, "c_var", 1)
                says("c_rms", act.activation(crs[:, :], PS[:, 3, 0:NT], ACT.Sqrt, scale=1.0 / 256, bias=epsb[:, :]))
                wait(act, L, "c_norm", 1)
                for c in range(2):
                    ins = act.activation(cacc[:, c, :], cacc[:, c, :], ACT.Silu,
                                         scale=pars[:, LNG + c:LNG + c + 1], bias=pars[:, LNB + c:LNB + c + 1])
                says("c_silu", ins)
                wait(act, L, "c_silu", 1)
                says("c_hi", act.activation(cp_hi[:, :, :], cacc[:, :, :], ACT.Copy))
                wait(act, L, "pool_y", 1)
                says("pl_hi", act.activation(pl_hi[:, :, :], pw[:, :, :], ACT.Copy))
                wait(act, L, "c_out", 1)
                says("c_ohi", act.activation(h_hi[:, 0:2, :], PS[:, 4:6, 0:NT], ACT.Copy))
                wait(act, L, "unit_done", u0 + N_IN)
                for c in range(2):
                    ins = act.activation(h_hi[:, 2 + c, :], PS[:, 6 + c, 0:NT], ACT.Copy,
                                         scale=pars[:, PSC + c:PSC + c + 1])
                says("pl_ohi", ins)
                for m in range(18, 26):
                    split(L, u0 + m)

            act.wait_ge(inputs, 16 * 4)
            act.wait_ge(setup, 1)
            for u in range(2):
                act.wait_ge(raw_full[u], 16)
                act.activation(w_hi[:, u, :], raw[:, u, :], ACT.Copy).then_inc(sem["w_hi"], 1)
            for d in range(KD):
                act.activation(x_hi[:, d, :], h[:, d, :], ACT.Copy,
                               scale=pars[:, PRE1 + d:PRE1 + d + 1]).then_inc(sem["x_hi"], 1)
                if d >= 4:
                    act.wait_ge(sem["mm_pre"], d - 3)
                act.activation(sq_pre[:, d % 4, :], h[:, d, :], ACT.Square).then_inc(sem["sq_pre"], 1)
            act.wait_ge(sem["mm_pre"], KD)
            act.activation(rstd[:, :], PS[:, 7, 0:NT], ACT.Sqrt, scale=1.0 / D,
                           bias=epsb[:, :]).then_inc(sem["rms_pre"], 1)
            with act.Fori(0, DEPTH) as L:
                ffn(L, 0, 0)
                post(L, 0, PREM)
                mixer(L)
                post(L, 1, PRE2)
                ffn(L, U_FFN2, KF)
                post(L, 2, PRE1N)
            counted()

        @block.vector
        def _(dve):
            tt, ts, stt = dve.tensor_tensor, dve.tensor_scalar, dve.scalar_tensor_tensor

            def split(L, u, i=0, turns=1):
                raw_ready(dve, L, u, i)
                split_free(dve, L, u, i)
                dve.wait_ge(sem["w_hi"], L * UNITS + i * RAW + (u + 1))
                says("w_lo", tt(w_lo[:, u % SPLIT, :], raw[:, u % RAW, :],
                                w_hi[:, u % SPLIT, :].bitcast(F32), AL.subtract), turns)

            def pre_lo(L, k, d, gain):
                wait(dve, L, "x_hi", k + d + 1)
                says("x_lo", stt(x_lo[:, d, :], h[:, d, :], pars[:, gain + d:gain + d + 1],
                                 x_hi[:, d, :].bitcast(F32), AL.mult, AL.subtract))

            def step(L, ins):
                says("step", ins)
                return made["step"]

            def after(L, k):
                wait(dve, L, "step", k)

            def post(L, n, gain, half, nxt):
                for d in range(KD):
                    wait(dve, L, "y_out", 8 * n + d + 1)
                    if d >= 4:
                        wait(dve, L, "mm_post", 8 * n + d - 3)
                    says("sq_post", tt(sq_post[:, d % 4, :], y[:, d, :], y[:, d, :], AL.mult))
                wait(dve, L, "rms_post", n + 1)
                after(L, step(L, dve.reciprocal(rstd_post[:, :], rstd_post[:, :])))
                scaled = []
                for d in range(KD + 2):
                    if d < KD:
                        scaled.append(step(L, stt(y[:, d, :], y[:, d, :], pars[:, gain + d:gain + d + 1],
                                                  rstd_post[:, :], AL.mult, AL.mult)))
                    if 0 < d <= KD:
                        after(L, scaled[d - 1])
                        says("h_new", stt(h[:, d - 1, :], y[:, d - 1, :], half, h[:, d - 1, :],
                                          AL.mult, AL.add))
                    if d > 1:
                        pre_lo(L, 8 * n, d - 2, nxt)
                wait(dve, L, "rms_pre", n + 1)
                says("rstd", dve.reciprocal(rstd[:, :], rstd[:, :]))

            def ffn(L, n, u0, f0):
                def gate(f, i=0, turns=1):
                    wait(dve, L, "unit_done", i * RAW + (u0 + 2 * f + 1))
                    if not isinstance(i, int):
                        wait(dve, L, "mid", i * 3 + (f0 + f - 2)) if f0 + f - 2 >= 0 and f > 2 else \
                            wait(dve, L, "mid", i * 3 + (f0 + max(f - 2, 0)))
                    says("gs", tt(gs[:, f % 3, :], PS[:, 2 * (f % 3), 0:NT], rstd[:, :], AL.mult), turns)

                def up(f, i=0, turns=1):
                    wait(dve, L, "unit_done", i * RAW + (u0 + 2 * f + 2))
                    wait(dve, L, "h_lo", i * 3 + (f0 + max(f - 2, 0)))
                    says("us", tt(us[:, f % 3, :], PS[:, 2 * (f % 3) + 1, 0:NT], rstd[:, :], AL.mult), turns)

                def lo(f, k, i=0, turns=1):
                    wait(dve, L, "h_hi", i * 3 + (f0 + f + 1))
                    if isinstance(k, int):
                        out, hi = h_lo[:, k, :], h_hi[:, k, :]
                    else:
                        out, hi = h_lo[:, bass.ds(k, 1), :], h_hi[:, bass.ds(k, 1), :]
                    says("h_lo", tt(out, us[:, f % 3, :], hi.bitcast(F32), AL.subtract), turns)

                split(L, u0 + 2)
                wait(dve, L, "rstd", n)
                gate(0)
                split(L, u0 + 3)
                up(0)
                with dve.Fori(0, ffn_loop) as i:
                    for f in range(1, 4):
                        split(L, u0 + 2 * f + 2, i, ffn_loop)
                        gate(f, i, ffn_loop)
                        split(L, u0 + 2 * f + 3, i, ffn_loop)
                        lo(f - 1, i * 3 + (f - 1), i, ffn_loop)
                        up(f, i, ffn_loop)
                split(L, u0 + 46)
                lo(KF - 1, KF - 1)
                split(L, u0 + 47)
                with dve.Fori(0, 3) as i:
                    for k in range(48, 54):
                        split(L, u0 + k, i, 3)
                split(L, u0 + 66)
                split(L, u0 + 67)

            def mixer(L):
                u0 = U_MIX
                perms, ropes = [0], [0]

                def chunk(m, *outs):
                    wait(dve, L, "unit_done", u0 + m + 1)
                    for n, (out, src, by) in enumerate(outs):
                        ins = stt(out, src, by[0], by[1], AL.mult, AL.mult)
                    says("chunk", ins)

                def plain(m, out):
                    chunk(m, (out, PS[:, m % 2, 0:NT], (1.0, rstd[:, :])))

                def rope(x, bank, own=None):
                    perms[0] += 1
                    wait(dve, L, "perm", perms[0])
                    tmp = rtmp[:, ropes[0] % 2, :]
                    if ropes[0] >= 2:
                        wait(dve, L, "rope", ropes[0] - 1)
                    tt(tmp, PS[:, bank, 0:NT], con[:, C_SIN:C_SIN + NT], AL.mult)
                    b = step(L, tt(x, x if own is None else own, con[:, C_COS:C_COS + NT], AL.mult))
                    after(L, b)
                    ropes[0] += 1
                    says("rope", tt(x, x, tmp, AL.add))

                split(L, u0 + 2)
                wait(dve, L, "rstd", 1)
                plain(0, qi[:, 0, :])
                split(L, u0 + 3)
                plain(1, qi[:, 1, :])
                split(L, u0 + 4)
                plain(2, kiw[:, :])
                rope(qi[:, 0, :], 2)
                rope(qi[:, 1, :], 3)
                split(L, u0 + 5)
                plain(3, ak[:, :])
                rope(ki[:, :], 5, own=PS[:, 4, 0:NT])
                wait(dve, L, "wi_t", 1)
                says("wi_w", dve.tensor_copy(wi[:, :, :], PS[:, 6, 0:256].rearrange(
                    "p (a b) -> p a b", a=2)[:, :, 64:64 + IH]))
                says("wi_mask", tt(w4[:, :].rearrange("p (a b) -> p a b", a=NB),
                                   kiw[:, NP:].unsqueeze(2).to_broadcast([128, NB, IH]),
                                   con[:, C_WIM:C_WIM + 32].rearrange("p (a b) -> p a b", a=NB), AL.mult))
                split(L, u0 + 6)
                plain(4, av[:, :])
                rope(ak[:, :], 7)
                wait(dve, L, "wi_x", 1)
                tt(wx[:, :], PS[0:32, 2, 0:64], con[0:32, C_WXM:C_WXM + 64], AL.mult)
                wait(dve, L, "swap", 1)
                flat = LQ[:, :, :].rearrange("p a b -> p (a b)")
                for half in range(2):
                    rows = slice(64 * half, 64 * half + 64)
                    dve.tensor_copy(kn[rows, :], ki[rows, NP + half:NT:2])
                    for hd in range(IH):
                        own = hd % 2 == half
                        src = qi[rows, hd // 2, NP + half:NT:2] if own else \
                            PS[rows, 3, (hd // 2) * NB + half:(hd // 2) * NB + NB:2]
                        ins = dve.tensor_copy(flat[rows, 4 * half + hd:4 * half + hd + 121:40], src)
                says("lq", ins)
                split(L, u0 + 7)
                plain(5, aq[:, 0, :])
                wait(dve, L, "wi_w", 1)
                for blk, (acc, r, c0) in enumerate(((wk1, relu, C_CA1), (wk0, relu0, C_CA0))):
                    wait(dve, L, "idx_relu", 2 * blk + 2)
                    seen = con[:, c0:c0 + acc.shape[1]]
                    for hd in range(IH):
                        k = step(L, stt(acc[:, :], r[:, (hd % 2) * 2 + hd // 2, :],
                                        wi[:, 1 - blk, hd:hd + 1], seen, AL.mult, AL.add))
                        after(L, k)
                        seen = acc[:, :]
                split(L, u0 + 8)
                plain(6, aq[:, 1, :])
                rope(aq[:, 0, :], 2)
                split(L, u0 + 9)
                plain(7, aq[:, 2, :])
                wait(dve, L, "idx_s", 1)
                dve.tensor_copy(X[:, 0:PAST], PS[0:64, 4:6, :].rearrange("p a b -> p (a b)"))
                says("idx_x", dve.tensor_copy(X[:, PAST:], PS[0:64, 6, 0:1]))
                rope(aq[:, 1, :], 7)
                split(L, u0 + 10)
                plain(8, aq[:, 3, :])
                rope(aq[:, 2, :], 2)
                split(L, u0 + 11)
                half_ = 0.5
                plain_cv = lambda m, c: chunk(m, (cv[:, c, :], PS[:, m % 2, 0:NT], (half_, rstd[:, :])))
                plain_cv(9, 0)
                rope(aq[:, 3, :], 3)
                wait(dve, L, "rope", 8)
                flat = LA[:, :, :].rearrange("p a b -> p (a b)")
                for j in range(4):
                    ins = dve.tensor_copy(flat[0:64, j * NB:j * NB + 456:65], aq[0:64, j, NP:])
                    ins = dve.tensor_copy(flat[64:128, (4 + j) * NB:(4 + j) * NB + 456:65], aq[64:128, j, NP:])
                says("la", ins)
                split(L, u0 + 12)
                plain(10, cg[:, 0, :])
                split(L, u0 + 13)
                plain_cv(11, 1)
                def glu(c):
                    wait(dve, L, "tanh", c + 1)
                    if c == 0:
                        dve.wait_ge(state_full, L * 32 + 32)
                    stt(gp[:, c, CK - 1:], cg[:, c, 0:NP], 1.0, cv[:, c, 0:NP], AL.add, AL.mult)
                    says("glu", stt(stc[:, c, :, CK - 1], cg[:, c, NP:], 1.0, cv[:, c, NP:], AL.add, AL.mult))

                glu(0)
                split(L, u0 + 14)
                plain(12, cg[:, 1, :])
                split(L, u0 + 15)
                glu(1)
                for c in range(2):
                    wait(dve, L, "unit_done", u0 + 13 + c + 1)
                    p = PS[:, (13 + c) % 2, 0:NT]
                    tt(pp[:, c, PB:], p[:, 0:NP], rstd[:, 0:NP], AL.mult)
                    tt(stp[:, c, :, PB], p[:, NP:], rstd[:, NP:], AL.mult)
                    says("chunk", tt(xp[:, c, :], p, rstd[:, :], AL.mult))
                    split(L, u0 + 16 + c)
                wait(dve, L, "chunk", 15)
                for g in range(4):
                    rows, w = slice(64 * (g % 2), 64 * (g % 2) + 64), 2 << g
                    ins = dve.tensor_reduce(pw[rows, g // 2, NP:], stp[rows, g // 2, :, PB + 1 - w:], AX.X, AL.add)
                says("pool_x", ins)

                for r in range(TOPK_P // 8):
                    for work, top in ((wk1, best), (wk0, best0)):
                        dve.max(top[:, :], work[:, :])
                    dve.drain()
                    for work, top in ((wk1, best), (wk0, best0)):
                        dve.match_replace(work[:, :], top[:, :], work[:, :], TAKEN)
                    dve.drain()
                a = step(L, ts(bias1[:, :], wk1[:, :], TAKEN / 2, -BIG, AL.is_gt, AL.mult))
                b = step(L, ts(bias0[:, :], wk0[:, :], TAKEN / 2, -BIG, AL.is_gt, AL.mult))
                after(L, a)
                step(L, tt(bias1[:, :], bias1[:, :], con[:, C_CA1:C_CA1 + 256], AL.add))
                after(L, b)
                after(L, step(L, tt(bias0[:, :], bias0[:, :], con[:, C_CA0:C_CA0 + 128], AL.add)))

                def masked(j):
                    wait(dve, L, "s_p", j + 1)
                    if j >= 2:
                        wait(dve, L, "p_t", 2 * j - 2)
                    ks = []
                    for a in range(2):
                        bank = 2 + 2 * (j % 2) + a
                        tt(sp_[:, j % 2, a, 0:256], PS[:, bank, 0:256], bias1[:, :], AL.add)
                        ks.append(step(L, tt(sp_[:, j % 2, a, 256:384], PS[:, bank, 256:384], bias0[:, :], AL.add)))
                    says("s_out", dve.nop()) if False else None
                    for a in range(2):
                        after(L, ks[a])
                        dve.reduce_max(spm[:, j % 2, 2 * a:2 * a + 1], sp_[:, j % 2, a, 0:256], AX.X)
                        k = step(L, dve.reduce_max(spm[:, j % 2, 2 * a + 1:2 * a + 2], sp_[:, j % 2, a, 256:384], AX.X))
                    after(L, k)
                    says("s_masked", ts(spm[:, j % 2, :], spm[:, j % 2, :], -SCALE, None, AL.mult))

                def norm(j):
                    wait(dve, L, "p_exp", j + 1)
                    after(L, step(L, dve.reciprocal(sps[:, j % 2, :], sps[:, j % 2, :])))
                    for a in range(2):
                        for b, (lo, hi) in enumerate(((0, 256), (256, 384))):
                            t = sp_[:, j % 2, a, lo:hi]
                            ins = ts(t, t, sps[:, j % 2, 2 * a + b:2 * a + b + 1], None, AL.mult)
                    says("p_norm", ins)

                masked(0)
                masked(1)
                for j in range(4):
                    norm(j)
                    if j < 2:
                        masked(j + 2)
                    wait(dve, L, "o_hi", j + 1)
                    says("o_lo", tt(h_lo[:, 4 + j, 0:NP], PS[:, j % 2, 0:NP],
                                    h_hi[:, 4 + j, 0:NP].bitcast(F32), AL.subtract))

                for r in range(TOPK_S // 8):
                    dve.max(bests[:, :], X[:, :])
                    dve.drain()
                    dve.match_replace(X[:, :], bests[:, :], X[:, :], TAKEN)
                    dve.drain()
                after(L, step(L, ts(bias_s[:, :], X[:, :], TAKEN / 2, -BIG, AL.is_gt, AL.mult)))
                wait(dve, L, "s_s", 1)
                tt(psm[:, 0:PAST], PS[0:64, 4:6, :].rearrange("p a b -> p (a b)"), bias_s[:, 0:PAST], AL.add)
                after(L, step(L, tt(psm[:, PAST:], PS[0:64, 6, 0:1], bias_s[:, PAST:], AL.add)))
                after(L, step(L, dve.reduce_max(smx[:, 0:1], psm[:, :], AX.X)))
                says("s_smax", ts(smx[:, 1:2], smx[:, 0:1], -SCALE, None, AL.mult))
                wait(dve, L, "p_sexp", 1)
                after(L, step(L, dve.reciprocal(smx[:, 3:4], smx[:, 2:3])))
                says("p_snorm", ts(psm[:, :], psm[:, :], smx[:, 3:4], None, AL.mult))
                wait(dve, L, "p_snorm", 1)
                says("dg", ts(dg[:, :], con[0:64, C_ID:C_ID + 64], psm[:, PAST:], None, AL.mult))
                wait(dve, L, "o_st", 1)
                after(L, step(L, tt(t2[:, :, :], PS[:, 0, 0:64].rearrange("p (a b) -> p a b", a=NH),
                                    av[:, NP:].unsqueeze(1).to_broadcast([128, NH, NB]), AL.mult)))
                for half in range(2):
                    rows = slice(64 * half, 64 * half + 64)
                    old = PS[rows, 6, 0:256].rearrange("p (b r) -> p r b", r=32)
                    ins = tt(ms[rows, :, :], old[:, 4 * half:4 * half + 4, :], t2[rows, 4 * half:4 * half + 4, :], AL.add)
                says("o_ms", ins)
                wait(dve, L, "o_shi", 1)
                says("o_slo", tt(h_lo[:, 4:8, NP:], ms[:, :, :], h_hi[:, 4:8, NP:].bitcast(F32), AL.subtract))

                wait(dve, L, "glu", 2)
                last = [None, None]
                for k in range(CK):
                    for c in range(2):
                        w = pars[:, DW + CK * c + k:DW + CK * c + k + 1]
                        if k == 0:
                            ins = ts(cacc[:, c, 0:NP], gp[:, c, 0:NP], w, pars[:, DWB + c:DWB + c + 1], AL.mult, AL.add)
                        else:
                            after(L, last[c])
                            ins = stt(cacc[:, c, 0:NP], gp[:, c, k:k + NP], w, cacc[:, c, 0:NP], AL.mult, AL.add)
                        last[c] = step(L, ins)
                for c in range(2):
                    last[c] = step(L, tt(ctmp[:, c, :, :], stc[:, c, :, :],
                                         pars[:, DW + CK * c:DW + CK * (c + 1)].unsqueeze(1).to_broadcast(
                                             [128, NB, CK]), AL.mult))
                for c in range(2):
                    after(L, last[c])
                    last[c] = step(L, dve.tensor_reduce(cacc[:, c, NP:], ctmp[:, c, :, :], AX.X, AL.add))
                for c in range(2):
                    after(L, last[c])
                    ins = ts(cacc[:, c, NP:], cacc[:, c, NP:], pars[:, DWB + c:DWB + c + 1], None, AL.add)
                says("conv", ins)
                wait(dve, L, "c_sum", 1)
                for c in range(2):
                    ins = stt(cacc[:, c, :], PS[:, 2, 0:NT], -1.0 / 256, cacc[:, c, :], AL.mult, AL.add)
                says("c_cent", ins)
                wait(dve, L, "c_rms", 1)
                after(L, step(L, dve.reciprocal(crs[:, :], crs[:, :])))
                for c in range(2):
                    ins = tt(cacc[:, c, :], cacc[:, c, :], crs[:, :], AL.mult)
                says("c_norm", ins)
                wait(dve, L, "c_hi", 1)
                says("c_lo", tt(cp_lo[:, :, :], cacc[:, :, :], cp_hi[:, :, :].bitcast(F32), AL.subtract))
                wait(dve, L, "pl_hi", 1)
                says("pl_lo", tt(pl_lo[:, :, :], pw[:, :, :], pl_hi[:, :, :].bitcast(F32), AL.subtract))
                wait(dve, L, "c_ohi", 1)
                says("c_olo", tt(h_lo[:, 0:2, :], PS[:, 4:6, 0:NT], h_hi[:, 0:2, :].bitcast(F32), AL.subtract))
                wait(dve, L, "pl_ohi", 1)
                for c in range(2):
                    ins = stt(h_lo[:, 2 + c, :], PS[:, 6 + c, 0:NT], pars[:, PSC + c:PSC + c + 1],
                              h_hi[:, 2 + c, :].bitcast(F32), AL.mult, AL.subtract)
                says("pl_olo", ins)
                for m in range(18, 26):
                    split(L, u0 + m)

            for t, name in ((LA, "unit_done"), (LQ, "gs"), (gp, "us"), (pp, "mid"), (osb, "h_lo")):
                flat = t[:].rearrange("p a b -> p (a b)")
                dve.memset(flat, 0.0).then_inc(sem[name], 1)
            dve.memset(epsb[:, :], EPS).then_inc(setup, 1)
            dve.wait_ge(inputs, 16 * 4)
            for u in range(2):
                dve.wait_ge(raw_full[u], 16)
                dve.wait_ge(sem["w_hi"], u + 1)
                tt(w_lo[:, u, :], raw[:, u, :], w_hi[:, u, :].bitcast(F32), AL.subtract).then_inc(sem["w_lo"], 1)
            for d in range(KD):
                dve.wait_ge(sem["x_hi"], d + 1)
                stt(x_lo[:, d, :], h[:, d, :], pars[:, PRE1 + d:PRE1 + d + 1],
                    x_hi[:, d, :].bitcast(F32), AL.mult, AL.subtract).then_inc(sem["x_lo"], 1)
            dve.wait_ge(sem["rms_pre"], 1)
            dve.reciprocal(rstd[:, :], rstd[:, :]).then_inc(sem["rstd"], 1)
            with dve.Fori(0, DEPTH) as L:
                ffn(L, 0, 0, 0)
                post(L, 0, POST1, 0.5, PREM)
                mixer(L)
                post(L, 1, POSTM, 1.0, PRE2)
                ffn(L, 2, U_FFN2, KF)
                post(L, 2, POST2, 0.5, PRE1N)
                dve.sem_inc(sem["step"], SIGNALS["step"] - made["step"])
                made["step"] = SIGNALS["step"]
            made["w_lo"] = made["w_lo"]
            counted()

        @block.tensor
        def _(pe):
            def three(out, w, cols, hi, lo, start, stop):
                pe.matmul(out, w_hi[:, w, cols], hi, start=start, stop=False)
                pe.matmul(out, w_hi[:, w, cols], lo, start=False, stop=False)
                return pe.matmul(out, w_lo[:, w, cols], hi, start=False, stop=stop)

            def split_ready(L, u, i=0):
                pe.wait_ge(sem["w_lo"], L * UNITS + i * RAW + (u + 1))

            def col(k):
                return slice(128 * k, 128 * k + 128)

            def rows_by_k(out, u, xh, xl, each=None):
                for k in range(KD):
                    if each is not None:
                        each(k)
                    ins = three(out, u % SPLIT, col(k), xh[:, k, :], xl[:, k, :], k == 0, k == KD - 1)
                return ins

            def sums(L, n, sq, name, done, bank, each=None):
                for d in range(KD):
                    wait(pe, L, name, 8 * n + d + 1)
                    says(done, pe.matmul(PS[:, bank, 0:NT], ones, sq[:, d % 4, :],
                                         start=(d == 0), stop=(d == KD - 1)))

            def norms(L, n):
                sums(L, n, sq_post, "sq_post", "mm_post", 0)
                sums(L, n, sq_pre, "sq_pre", "mm_pre", 7)

            def ffn(L, n, u0, f0):
                def gate_up(f, i=0, turns=1, each=None):
                    for part in range(2):
                        u = u0 + 2 * f + part
                        split_ready(L, u, i)
                        if not isinstance(i, int):
                            wait(pe, L, ("gs", "us")[part], i * 3 + (f0 + max(f - 2, 0)))
                        ins = rows_by_k(PS[:, 2 * (f % 3) + part, 0:NT], u, x_hi, x_lo,
                                        each if part == 0 else None)
                        says("unit_done", ins, turns)

                def down(k, at_k, i=0, turns=1, order=range(KD), before={}, start=False, stop=False):
                    u = u0 + 2 * KF + k
                    split_ready(L, u, i)
                    wait(pe, L, "h_lo", i * 6 + (f0 + k + 1))
                    hi, lo = (t[:, at_k, :] if isinstance(at_k, int) else t[:, bass.ds(at_k, 1), :]
                              for t in (h_hi, h_lo))
                    for d in order:
                        if d in before:
                            wait(pe, L, "us", before[d])
                        ins = three(PS[:, d, 0:NT], u % SPLIT, col(d), hi, lo, start, stop)
                        if stop and d < KD - 1:
                            says("y_done", ins)
                    says("unit_done", ins, turns)

                gate_up(0, each=lambda k: wait(pe, L, "x_lo", 8 * (n - 1) + k + 1))
                with pe.Fori(0, ffn_loop) as i:
                    for f in range(1, 4):
                        gate_up(f, i, ffn_loop)
                down(0, 0, order=(6, 7, 2, 3, 4, 5, 0, 1), start=True,
                     before={2: f0 + 20, 4: f0 + 21, 0: f0 + 22})
                with pe.Fori(0, 3) as i:
                    for k in range(1, 7):
                        down(k, i * 6 + k, i, 3)
                for k in range(19, KF):
                    down(k, k, stop=(k == KF - 1))

            def mixer(L):
                u0 = U_MIX

                def unit(m, each=None):
                    split_ready(L, u0 + m)
                    if m >= 2:
                        wait(pe, L, "chunk", m - 1)
                    says("unit_done", rows_by_k(PS[:, m % 2, 0:NT], u0 + m, x_hi, x_lo, each))

                def perm(m, x, bank, which=C_PERM):
                    wait(pe, L, "chunk", m + 1)
                    return pe.matmul(PS[:, bank, 0:NT], con[:, which:which + 128], x, start=True, stop=True)

                unit(0, each=lambda k: wait(pe, L, "x_lo", k + 1))
                unit(1)
                unit(2)
                says("perm", perm(0, qi[:, 0, :], 2))
                says("perm", perm(1, qi[:, 1, :], 3))
                unit(3)
                perm(2, kiw[:, :], 4, C_DUP)
                says("perm", perm(2, kiw[:, :], 5, C_DUPP))
                for b in range(2):
                    ins = pe.transpose(PS[:, 6, 128 * b:128 * b + 128], kiw[:, 128 * b:128 * b + 128], ident)
                says("wi_t", ins)
                unit(4)
                says("perm", perm(3, ak[:, :], 7))
                wait(pe, L, "rope", 1)
                wait(pe, L, "wi_mask", 1)
                says("wi_x", pe.matmul(PS[0:32, 2, 0:64], w4[:, :], con[:, C_ONE:C_ONE + 64], start=True, stop=True))
                wait(pe, L, "rope", 2)
                for c in range(2):
                    ins = pe.matmul(PS[:, 3, NB * c:NB * c + NB], con[:, C_SWAP:C_SWAP + 128], qi[:, c, NP:],
                                    start=True, stop=True)
                says("swap", ins)
                unit(5)
                wait(pe, L, "rope", 3)
                wait(pe, L, "wi_w", 1)
                for hf in range(2):
                    rows = slice(64 * hf, 64 * hf + 64)
                    for c in range(2):
                        ins = pe.matmul(PS[:, 4 + hf, 256 * c:256 * c + 256], qi[rows, c, 128:256], ki[rows, 0:256],
                                        start=True, stop=True)
                    says("idx_p", ins)
                wait(pe, L, "rope", 4)
                for hf in range(2):
                    rows = slice(64 * hf, 64 * hf + 64)
                    for c in range(2):
                        ins = pe.matmul(PS[:, 6 + hf, 128 * c:128 * c + 128], qi[rows, c, 0:128], ki[rows, 0:128],
                                        start=True, stop=True)
                    says("idx_p", ins)
                wait(pe, L, "lq", 1)
                for b in range(2):
                    ins = pe.transpose(PS[:, 3, 128 * b:128 * b + 128], av[:, 128 * b:128 * b + 128], ident)
                says("v_t", ins)
                unit(6)
                says("perm", perm(5, aq[:, 0, :], 2))
                pe.wait_ge(kx_full, L * (16 * NB * NPG) + 16 * NB * NPG)
                for c in range(2):
                    wait(pe, L, "idx_relu", c + 1)
                    for m in range(4):
                        pe.matmul(PS[0:32, 4 + c, :], LQ[:, m, :], kx[:, m, 512 * c:512 * c + 512],
                                  start=(m == 0), stop=(m == 3))
                wait(pe, L, "idx_relu", 3)
                for m in range(4):
                    ins = pe.matmul(PS[0:32, 6, 0:1], LQ[:, m, :], kn[:, m:m + 1], start=(m == 0), stop=(m == 3))
                says("idx_d", ins)
                unit(7)
                wait(pe, L, "idx_relu", 4)
                says("perm", perm(6, aq[:, 1, :], 7))
                wait(pe, L, "idx_dr", 1)
                for c in range(2):
                    pe.matmul(PS[0:64, 4 + c, :], wx[:, :], rd[:, 512 * c:512 * c + 512], start=True, stop=True)
                says("idx_s", pe.matmul(PS[0:64, 6, 0:1], wx[:, :], rd[:, PAST:], start=True, stop=True))
                unit(8)
                wait(pe, L, "rope", 5)
                says("perm", perm(7, aq[:, 2, :], 2))
                unit(9)
                wait(pe, L, "v_nat", 1)
                says("perm", perm(8, aq[:, 3, :], 3))
                for m in range(10, 15):
                    unit(m)

                def scores(j):
                    if j == 0:
                        wait(pe, L, "rope", 8)
                        wait(pe, L, "idx_x", 1)
                    if j >= 2:
                        wait(pe, L, "s_masked", j - 1)
                    for a in range(2):
                        rows = slice(64 * a, 64 * a + 64)
                        bank = 2 + 2 * (j % 2) + a
                        pe.matmul(PS[:, bank, 0:256], aq[rows, j, 128:256], ak[rows, 0:256], start=True, stop=True)
                        ins = pe.matmul(PS[:, bank, 256:384], aq[rows, j, 0:128], ak[rows, 0:128],
                                        start=True, stop=True)
                    says("s_p", ins)

                scores(0)
                scores(1)
                for j in range(4):
                    wait(pe, L, "p_norm", j + 1)
                    for a in range(2):
                        if j:
                            wait(pe, L, "p_tc", 2 * j - 1 + a)
                        p = sp_[:, j % 2, a, :]
                        for n, c in enumerate((256, 0, 128)):
                            ins = pe.transpose(PS[:, 6 + a, 128 * n:128 * n + 128], p[:, c:c + 128], ident)
                        says("p_t", ins)
                    if j < 2:
                        scores(j + 2)
                    if j >= 2:
                        wait(pe, L, "o_lo", j - 1)
                    else:
                        wait(pe, L, "chunk", 15)
                    for a in range(2):
                        wait(pe, L, "p_tc", 2 * j + a + 1)
                        out = PS[64 * a:64 * a + 64, j % 2, :]
                        pe.matmul(out[:, 0:256], vn[:, 0, 64 * a:64 * a + 64], pT[:, a, 0:256], start=True, stop=False)
                        ins = pe.matmul(out[:, 128:256], vn[:, 1, 64 * a:64 * a + 64], pT[:, a, 256:384],
                                        start=False, stop=True)
                    says("o_p", ins)

                wait(pe, L, "la", 1)
                wait(pe, L, "s_masked", 4)
                wait(pe, L, "p_tc", 8)
                for b in range(NB):
                    pe.wait_ge(kv_full[b % KV], L * 512 + 128 * (b // KV + 1))
                    for c in range(2):
                        ins = pe.matmul(PS[0:64, 4 + c, :], LA[:, b, :], kv[:, b % KV, 512 * c:512 * c + 512],
                                        start=(b == 0), stop=(b == NB - 1))
                    says("k_used", ins)
                for b in range(NB):
                    ins = pe.matmul(PS[0:64, 6, 0:1], LA[:, b, :], ak[:, NP + b:NP + b + 1],
                                    start=(b == 0), stop=(b == NB - 1))
                says("s_s", ins)
                wait(pe, L, "dg", 1)
                wait(pe, L, "o_lo", 3)
                pe.matmul(PS[:, 0, 0:64], ones[0:64, :], dg[:, :], start=True, stop=True)
                for c in range(NPG):
                    ins = pe.transpose(PS[:, 7, 64 * c:64 * c + 64], psm[:, 128 * c:128 * c + 128], ident[0:64, 0:64])
                says("p_st", ins)
                wait(pe, L, "p_stc", 1)
                for b in range(NB):
                    pe.wait_ge(kv_full[b % KV], L * 512 + 256 + 128 * (b // KV + 1))
                    q = 32 * (b % 4)
                    for c in range(NPG):
                        ins = pe.matmul(PS[q:q + 8, 2 + b // 4, 0:128], pTs[:, c, b::8],
                                        kv[:, b % KV, 128 * c:128 * c + 128], start=(c == 0), stop=(c == NPG - 1))
                    says("v_used", ins)
                wait(pe, L, "o_sc", 1)
                for c in range(2):
                    ins = pe.transpose(PS[:, 6, 128 * c:128 * c + 128], osb[:, c, :], ident)
                says("o_st", ins)

                wait(pe, L, "conv", 1)
                for c in range(2):
                    ins = pe.matmul(PS[:, 2, 0:NT], ones, cacc[:, c, :], start=(c == 0), stop=(c == 1))
                says("c_sum", ins)
                wait(pe, L, "c_sq", 1)
                for c in range(2):
                    ins = pe.matmul(PS[:, 3, 0:NT], ones, csq[:, c, :], start=(c == 0), stop=(c == 1))
                says("c_var", ins)
                split_ready(L, u0 + 15)
                w = (u0 + 15) % SPLIT
                wait(pe, L, "c_lo", 1)
                wait(pe, L, "s_smax", 1)
                for c in range(2):
                    for k in range(2):
                        ins = three(PS[:, 4 + c, 0:NT], w, col(2 * k + c), cp_hi[:, k, :], cp_lo[:, k, :],
                                    k == 0, k == 1)
                says("c_out", ins)
                wait(pe, L, "pl_lo", 1)
                wait(pe, L, "o_ms", 1)
                for c in range(2):
                    ins = three(PS[:, 6 + c, 0:NT], w, col(4 + c), pl_hi[:, c, :], pl_lo[:, c, :], True, True)
                says("unit_done", ins)
                wait(pe, L, "o_lo", 4)
                wait(pe, L, "o_slo", 1)
                wait(pe, L, "c_olo", 1)
                wait(pe, L, "pl_olo", 1)
                for o in range(KD):
                    split_ready(L, u0 + N_IN + o)
                    ins = rows_by_k(PS[:, o, 0:NT], u0 + N_IN + o, h_hi, h_lo)
                    says("unit_done", ins)

            pe.wait_ge(inputs, 16 * 4)
            for d in range(KD):
                pe.wait_ge(sem["sq_pre"], d + 1)
                pe.matmul(PS[:, 7, 0:NT], ones, sq_pre[:, d % 4, :], start=(d == 0),
                          stop=(d == KD - 1)).then_inc(sem["mm_pre"], 1)
            with pe.Fori(0, DEPTH) as L:
                ffn(L, 0, 0, 0)
                norms(L, 0)
                mixer(L)
                norms(L, 1)
                ffn(L, 2, U_FFN2, KF)
                norms(L, 2)
            counted()

        @block.gpsimd
        def _(pool):
            def pstep(L, ins):
                says("pstep", ins)
                wait(pool, L, "pstep", made["pstep"])

            def ffn(L, f0):
                def mid(f, i=0, turns=1):
                    wait(pool, L, "silu", i * 3 + (f0 + f + 1))
                    wait(pool, L, "us", i * 3 + (f0 + f + 1))
                    says("mid", pool.tensor_tensor(us[:, f % 3, :], gs[:, f % 3, :], us[:, f % 3, :], AL.mult), turns)

                mid(0)
                with pool.Fori(0, ffn_loop) as i:
                    for f in range(1, 4):
                        mid(f, i, ffn_loop)

            pool.dma_start(h[:, :, :], xT).then_inc(inputs, 16)
            pool.dma_start(pars[:, :], par[0]).then_inc(inputs, 16)
            pool.dma_start(con[:, :], cst).then_inc(inputs, 16)
            pool.dma_start(tab[:, :], ptab).then_inc(inputs, 16)
            pool.wait_ge(inputs, 64)
            pool.wait_ge(setup, 1)
            with pool.Fori(0, DEPTH) as L:
                pool.dma_start(stc[:, :, :, 0:CK - 1], scT[bass.ds(L, 1)].rearrange("a p c b k -> p (a c) b k")) \
                    .then_inc(state_full, 16)
                pool.dma_start(stp[:, :, :, 0:PB], spT[bass.ds(L, 1)].rearrange("a p c b k -> p (a c) b k")) \
                    .then_inc(state_full, 16)
                ffn(L, 0)
                out = lambda t: t[bass.ds(L, 1)].rearrange("a p n -> (a p) n")
                wait(pool, L, "rope", 4)
                pool.dma_start(out(okT), ak[:, :]).then_inc(stored, 16)
                pool.dma_start(out(ovT), av[:, :]).then_inc(stored, 16)
                pool.dma_start(out(okiT), ki[0:64, :]).then_inc(stored, 16)
                out4 = lambda t: t[bass.ds(L, 1)].rearrange("a p c b k -> p (a c) b k")
                wait(pool, L, "glu", 2)
                pool.dma_start(ocP[bass.ds(L, 1)].rearrange("a p c k -> p (a c) k"), gp[:, :, NP:]).then_inc(stored, 16)
                pool.dma_start(out4(ocS), stc[:, :, :, 1:]).then_inc(stored, 16)
                wait(pool, L, "pool_x", 1)
                pool.dma_start(opP[bass.ds(L, 1)].rearrange("a p c k -> p (a c) k"), pp[:, :, NP:]).then_inc(stored, 16)
                pool.dma_start(out4(opS), stp[:, :, :, 1:]).then_inc(stored, 16)
                add = lambda o, a, b: pool.tensor_tensor(o, a, b, AL.add)
                pstep(L, add(pa[:, 0:270], pp[:, 0, 0:270], pp[:, 0, 1:271]))
                add(pw[64:128, 0, 0:NP], pa[64:128, 12:12 + NP], pa[64:128, 14:14 + NP])
                pstep(L, pool.tensor_copy(pw[0:64, 0, 0:NP], pa[0:64, 14:14 + NP]))
                pstep(L, add(pa[:, 0:270], pp[:, 1, 0:270], pp[:, 1, 1:271]))
                pstep(L, add(pb[:, 0:268], pa[:, 0:268], pa[:, 2:270]))
                pstep(L, add(pa[:, 0:264], pb[:, 0:264], pb[:, 4:268]))
                add(pw[64:128, 1, 0:NP], pa[64:128, 0:NP], pa[64:128, 8:8 + NP])
                pstep(L, pool.tensor_copy(pw[0:64, 1, 0:NP], pa[0:64, 8:8 + NP]))
                pstep(L, pool.tensor_tensor(pw[:, :, :], pw[:, :, :],
                                            con[:, C_CNT:C_CNT + 2 * NT].rearrange("p (a b) -> p a b", a=2), AL.mult))
                says("pool_y", pool.tensor_tensor(pw[:, :, :], pw[:, :, :], xp[:, :, :], AL.subtract))
                pool.wait_ge(stored, L * 112 + 112)
                ffn(L, KF)
                wait(pool, L, "x_lo", 24)
                pool.dma_start(pars[:, :], par[bass.ds(L + 1, 1)].rearrange("a p n -> (a p) n")).then_inc(pars_full, 16)
                pool.wait_ge(pars_full, L * 16 + 16)
                pool.sem_inc(sem["pstep"], SIGNALS["pstep"] - made["pstep"])
                made["pstep"] = SIGNALS["pstep"]
            counted()
            pool.dma_start(yT, h[:, :, :]).then_inc(stored, 16)
            pool.wait_ge(stored, DEPTH * 112 + 16)


def _units(w):
    k, n = w.shape[0] // 128, w.shape[1] // 128
    return w.reshape(k, 128, n, 128).transpose(2, 1, 0, 3).reshape(n, 128, k * 128)


def _constants():
    c = np.zeros((128, NCONST), np.float32)
    r = np.arange(128)
    c[r, C_ID + r] = 1
    rot = r % 64
    for first in (C_PERM, C_DUPP):
        for row in range(128):
            if rot[row] < 16:
                src, sign = (row + 8, -1) if rot[row] < 8 else (row - 8, 1)
                c[src if first == C_PERM else src % 64, first + row] = sign
    c[r % 64, C_DUP + r] = 1
    c[(r + 64) % 128, C_SWAP + r] = 1
    c[:, C_ONE:C_ONE + 128] = 1
    pos = np.concatenate([np.arange(NP), np.full(NB, PAST)]).astype(np.float32)
    inv = np.float32(500000.0) ** (-np.arange(8, dtype=np.float32) * np.float32(2.0) / np.float32(16))
    ang = (pos[None, :] * inv[:, None].astype(np.float32)).astype(np.float32)
    c[:, C_COS:C_COS + NT] = 1
    for row in range(128):
        if rot[row] < 16:
            c[row, C_COS:C_COS + NT] = np.cos(ang[rot[row] % 8])
            c[row, C_SIN:C_SIN + NT] = np.sin(ang[rot[row] % 8])
    for g in range(4):
        cnt = np.minimum(2 << g, pos + 1)
        rows = slice(64 * (g % 2), 64 * (g % 2) + 64)
        c[rows, C_CNT + NT * (g // 2):C_CNT + NT * (g // 2) + NT] = 1 / cnt
    q = np.arange(128)
    c[:, C_CA0:C_CA0 + 128] = np.where(np.arange(128)[None, :] <= q[:, None], 0, -BIG)
    c[:, C_CA1:C_CA1 + 256] = np.where(np.arange(256)[None, :] <= 128 + q[:, None], 0, -BIG)
    for hd in range(IH):
        c[64 + hd, C_WIM + hd:C_WIM + 32:IH] = 1
    for b in range(NB):
        c[4 * b:4 * b + 4, C_WXM + b:C_WXM + 64:NB] = IH ** -0.5
    return c


def kernel(**inputs):
    import concourse.bacc as bacc
    from concourse.bass_utils import run_bass_kernel_spmd as run

    a = {k: np.asarray(v) for k, v in inputs.items()}
    n_phys = a["cache_k"].shape[1]
    wts = np.zeros((DEPTH * UNITS + TAIL, 128, 1024), np.float32)
    order = [np.arange(1536, 1664), np.arange(1664, 1792), None, np.arange(1280, 1408), np.arange(1408, 1536)]
    order += [768 + np.concatenate([np.arange(64 * j, 64 * j + 64), np.arange(64 * j + 256, 64 * j + 320)])
              for j in range(4)]
    order += [np.arange(128 * c, 128 * c + 128) for c in (0, 2, 1, 3)]
    order += [np.arange(512, 640), np.arange(640, 768)]
    mixed = np.concatenate([np.arange(512)] + [512 + o - 768 for o in order[5:9]])
    for layer in range(DEPTH):
        u = layer * UNITS
        for n, first in (("ffn1", u), ("ffn2", u + U_FFN2)):
            wts[first:first + 2 * KF:2] = _units(a[n + "_w_gate"][layer])
            wts[first + 1:first + 2 * KF:2] = _units(a[n + "_w_up"][layer])
            wts[first + 2 * KF:first + U_FFN] = a[n + "_w_down"][layer].reshape(KF, 128, D)
        w_in = a["w_in"][layer]
        for m, cols in enumerate(order):
            block = w_in[:, 1792:1860] if cols is None else w_in[:, cols]
            full = np.zeros((D, 128), np.float32)
            full[:, :block.shape[1]] = block
            wts[u + U_MIX + m] = _units(full)[0]
        misc = wts[u + U_MIX + 15]
        misc[:, 0:512] = a["conv_pw"][layer].reshape(2, 128, 256).transpose(1, 0, 2).reshape(128, 512)
        for g in range(4):
            at = 64 * (g % 2)
            misc[at:at + 64, 512 + 128 * (g // 2) + at:512 + 128 * (g // 2) + at + 64] = a["pool_w"][layer, g]
        wts[u + U_MIX + N_IN:u + U_FFN2] = _units(a["w_out"][layer][mixed])
    col = lambda v: v.reshape(-1, 128).T
    par = np.zeros((DEPTH + 1, 128, NPAR), np.float32)
    for layer in range(DEPTH):
        nxt = min(layer + 1, DEPTH - 1)
        parts = [col(a[n][layer]) for n in ("ffn1_norm_pre", "ffn1_norm_post", "mix_norm_pre", "mix_norm_post",
                                            "ffn2_norm_pre", "ffn2_norm_post")]
        parts += [col(a["ffn1_norm_pre"][nxt])]
        parts += [a["conv_dw"][layer].T.reshape(2, 128, CK).transpose(1, 0, 2).reshape(128, 2 * CK)]
        parts += [col(a[n][layer]) for n in ("conv_dw_bias", "conv_ln_gain", "conv_ln_bias", "pool_scale")]
        par[layer] = np.concatenate(parts, axis=1)
    x = np.concatenate([a["x_prompt"].reshape(NP, D), a["x_sample"].reshape(NB, D)])
    arrays = dict(
        xT=x.reshape(NT, KD, 128).transpose(2, 1, 0), wts=wts, par=par, cst=_constants(),
        ptab=a["page_table"].reshape(1, NB * NPG).astype(np.int32),
        kT=a["cache_k"].reshape(DEPTH, n_phys, PAGE, 128).transpose(0, 1, 3, 2),
        vC=a["cache_v"].reshape(DEPTH, n_phys, PAGE, 128),
        kxT=a["cache_kidx"].transpose(0, 1, 3, 2),
        scT=a["state_conv"].reshape(DEPTH, NB, CK - 1, 2, 128).transpose(0, 4, 3, 1, 2),
        spT=a["state_pool"].reshape(DEPTH, NB, PB, 2, 128).transpose(0, 4, 3, 1, 2))
    arrays = {k: np.ascontiguousarray(v) for k, v in arrays.items()}
    outs = dict(yT=(128, KD, NT), okT=(DEPTH, 128, NT), ovT=(DEPTH, 128, NT), okiT=(DEPTH, 64, NT),
                ocP=(DEPTH, 128, 2, CK - 1), ocS=(DEPTH, 128, 2, NB, CK - 1),
                opP=(DEPTH, 128, 2, PB), opS=(DEPTH, 128, 2, NB, PB))
    nc = bacc.Bacc("TRN2", target_bir_lowering=False, num_devices=1)
    args = [nc.dram_tensor("in_" + n, v.shape, mybir.dt.from_np(v.dtype), kind="ExternalInput").ap()
            for n, v in arrays.items()]
    args += [nc.dram_tensor("out_" + n, s, F32, kind="ExternalOutput").ap() for n, s in outs.items()]
    build(nc, *args)
    r = run(nc, [{"in_" + n: v for n, v in arrays.items()}], core_ids=[0]).results[0]
    g = {n: np.asarray(r["out_" + n]) for n in outs}
    yy = g["yT"].transpose(2, 1, 0).reshape(NT, D)
    k, v = (g[n].transpose(0, 2, 1).reshape(DEPTH, NT, 2, HD) for n in ("okT", "ovT"))
    ki = g["okiT"].transpose(0, 2, 1)
    hist_p = lambda t: t.transpose(0, 3, 2, 1).reshape(DEPTH, 1, t.shape[3], 256)
    hist_s = lambda t: t.transpose(0, 3, 4, 2, 1).reshape(DEPTH, NB, t.shape[4], 256)
    c = np.ascontiguousarray
    return (c(yy[:NP].reshape(1, NP, D)), c(yy[NP:].reshape(NB, 1, D)),
            c(k[:, :NP].reshape(DEPTH, 1, NP, 2, HD)), c(v[:, :NP].reshape(DEPTH, 1, NP, 2, HD)),
            c(ki[:, :NP].reshape(DEPTH, 1, NP, HD)), c(hist_p(g["ocP"])), c(hist_p(g["opP"])),
            c(k[:, NP:].reshape(DEPTH, NB, 1, 2, HD)), c(v[:, NP:].reshape(DEPTH, NB, 1, 2, HD)),
            c(ki[:, NP:].reshape(DEPTH, NB, 1, HD)), c(hist_s(g["ocS"])), c(hist_s(g["opS"])))
```
